# Optimizing a Trainium2 kernel written in Bass

```python
import jax
import jax.numpy as jnp
from jax import lax
import numpy as np

D_MODEL = 2048
BATCH = 1
SEQ = 256
DEPTH = 1
DEC_BATCH = 1
DEC_SEQ = 32
PAST_LEN = 128

CHUNK = 64
D_CONV = 1024
CONV_WIDTH = 31
N_HEADS = 16
N_KV_HEADS = 4
HEAD_DIM = 64
GROUP = N_HEADS // N_KV_HEADS
D_ATTN = N_HEADS * HEAD_DIM
KV_DIM = N_KV_HEADS * HEAD_DIM
D_MIX = D_CONV + D_ATTN
IN_COLS = 2 * D_CONV + D_ATTN + 2 * KV_DIM
ROT_DIM = HEAD_DIM // 4
ROPE_THETA = 500000.0
WINDOW = 128
WINDOW_CHUNKS = WINDOW // CHUNK
N_MEM = 256
MEM_HEADS = 4
MEM_HEAD_DIM = 128
D_MEM = MEM_HEADS * MEM_HEAD_DIM
PEER_HEADS = 8
N_KEYS = 128
N_EXPERTS = N_KEYS * N_KEYS
PEER_DK = 256
PEER_TOPK = 16
PEER_BLOCK = 256
EPS = 1e-6
NEG = -1e30

kernel_name = "hymba_conformer_swa_peer_stream_step"

def rmsnorm(x, g):
    xf = x.astype(jnp.float32)
    y = xf * lax.rsqrt(jnp.mean(xf * xf, axis=-1, keepdims=True) + EPS)
    return (y * g.astype(jnp.float32)).astype(x.dtype)

def layernorm(x, g, b):
    xf = x.astype(jnp.float32)
    mu = jnp.mean(xf, axis=-1, keepdims=True)
    var = jnp.mean(jnp.square(xf - mu), axis=-1, keepdims=True)
    y = (xf - mu) * lax.rsqrt(var + EPS) * g.astype(jnp.float32) + b.astype(jnp.float32)
    return y.astype(x.dtype)

def partial_rope(x, pos):
    half = ROT_DIM // 2
    inv_freq = jnp.power(jnp.float32(ROPE_THETA), -(2.0 * jnp.arange(half, dtype=jnp.float32)) / ROT_DIM)
    ang = pos.astype(jnp.float32)[:, None] * inv_freq[None, :]
    cos = jnp.cos(ang)[None, :, None, :]
    sin = jnp.sin(ang)[None, :, None, :]
    xr = x[..., :ROT_DIM].astype(jnp.float32)
    x1, x2 = xr[..., :half], xr[..., half:]
    rot = jnp.concatenate([x1 * cos - x2 * sin, x2 * cos + x1 * sin], axis=-1).astype(x.dtype)
    return jnp.concatenate([rot, x[..., ROT_DIM:]], axis=-1)

def sink_gqa_attention(q, k, v, sinks, mask):
    lead = q.shape[:-3]
    tq, hd = q.shape[-3], q.shape[-1]
    qg = q.reshape(lead + (tq, N_KV_HEADS, GROUP, hd))
    s = jnp.einsum('...qkgd,...skd->...kgqs', qg, k).astype(jnp.float32) * (hd ** -0.5)
    if mask is not None:
        s = jnp.where(mask, s, NEG)
    sink = jnp.broadcast_to(sinks.astype(jnp.float32).reshape(N_KV_HEADS, GROUP, 1, 1), s.shape[:-1] + (1,))
    p = jax.nn.softmax(jnp.concatenate([s, sink], axis=-1), axis=-1)[..., :-1]
    o = jnp.einsum('...kgqs,...skd->...qkgd', p.astype(v.dtype), v)
    return o.reshape(lead + (tq, N_HEADS, hd))

def swa_prompt(q, k, v, sinks):
    b, t = q.shape[:2]
    nc = t // CHUNK
    qc = q.reshape(b, nc, CHUNK, N_HEADS, HEAD_DIM)

    def band(a):
        ac = a.reshape(b, nc, CHUNK, N_KV_HEADS, HEAD_DIM)
        ap = jnp.pad(ac, ((0, 0), (WINDOW_CHUNKS, 0), (0, 0), (0, 0), (0, 0)))
        return jnp.concatenate([ap[:, j:j + nc] for j in range(WINDOW_CHUNKS + 1)], axis=2)

    kb, vb = band(k), band(v)
    offs = jnp.repeat(jnp.arange(WINDOW_CHUNKS + 1) - WINDOW_CHUNKS, CHUNK)
    key_chunk = jnp.arange(nc)[:, None] + offs[None, :]
    mask = (key_chunk >= 0)[None, :, None, None, None, :]
    o = sink_gqa_attention(qc, kb, vb, sinks, mask)
    return o.reshape(b, t, D_ATTN)

def conformer_conv(a, hist, dw_w, dw_b, ln_g, ln_b):
    glu = a[..., :D_CONV] * jax.nn.sigmoid(a[..., D_CONV:])
    xin = jnp.concatenate([hist.astype(glu.dtype), glu], axis=1)
    y = lax.conv_general_dilated(xin, dw_w[:, None, :].astype(xin.dtype), window_strides=(1,), padding='VALID',
                                 dimension_numbers=('NWC', 'WIO', 'NWC'), feature_group_count=D_CONV)
    y = jax.nn.silu(layernorm(y + dw_b, ln_g, ln_b))
    return y, xin[:, -(CONV_WIDTH - 1):]

def memory_kv(mem, norm_mem_g, w_ck, w_cv):
    b = mem.shape[0]
    mn = rmsnorm(mem, norm_mem_g)
    mk = (mn @ w_ck).reshape(b, -1, MEM_HEADS, MEM_HEAD_DIM)
    mv = (mn @ w_cv).reshape(b, -1, MEM_HEADS, MEM_HEAD_DIM)
    return mk, mv

def cross_attention(xn, mk, mv, w_cq, w_co):
    b, t = xn.shape[:2]
    q = (xn @ w_cq).reshape(b, t, MEM_HEADS, MEM_HEAD_DIM)
    s = jnp.einsum('bqhd,bshd->bhqs', q, mk).astype(jnp.float32) * (MEM_HEAD_DIM ** -0.5)
    p = jax.nn.softmax(s, axis=-1)
    o = jnp.einsum('bhqs,bshd->bqhd', p.astype(mv.dtype), mv).reshape(b, t, D_MEM)
    return o @ w_co

def peer_ffn(xn, w_q, sub_keys, u, v):
    b, t, d = xn.shape
    n = b * t
    xf = xn.reshape(n, d)
    q = (xf @ w_q).reshape(n, PEER_HEADS, 2, PEER_DK // 2)
    s = jnp.einsum('nhpd,hpkd->nhpk', q, sub_keys).astype(jnp.float32)
    sv, si = lax.top_k(s, PEER_TOPK)
    cand = (sv[:, :, 0, :, None] + sv[:, :, 1, None, :]).reshape(n, PEER_HEADS, PEER_TOPK * PEER_TOPK)
    cidx = (si[:, :, 0, :, None] * N_KEYS + si[:, :, 1, None, :]).reshape(n, PEER_HEADS, PEER_TOPK * PEER_TOPK)
    tv, tsel = lax.top_k(cand, PEER_TOPK)
    eidx = jnp.take_along_axis(cidx, tsel, axis=-1).reshape(n, PEER_HEADS * PEER_TOPK)
    g = jax.nn.softmax(tv, axis=-1).reshape(n, PEER_HEADS * PEER_TOPK).astype(xn.dtype)
    nb = -(-n // PEER_BLOCK)
    pad = nb * PEER_BLOCK - n
    xb = jnp.pad(xf, ((0, pad), (0, 0))).reshape(nb, PEER_BLOCK, d)
    ib = jnp.pad(eidx, ((0, pad), (0, 0))).reshape(nb, PEER_BLOCK, PEER_HEADS * PEER_TOPK)
    gb = jnp.pad(g, ((0, pad), (0, 0))).reshape(nb, PEER_BLOCK, PEER_HEADS * PEER_TOPK)

    def expert_block(args):
        xt, it, gt = args
        act = jax.nn.gelu(jnp.einsum('nd,ned->ne', xt, u[it]), approximate=False) * gt
        return jnp.einsum('ne,ned->nd', act, v[it])

    y = lax.map(expert_block, (xb, ib, gb)).reshape(nb * PEER_BLOCK, d)[:n]
    return y.reshape(b, t, d)

def layer_forward(h, pos, conv_hist, swa_k_hist, swa_v_hist, mem_k, mem_v,
                  norm_mix_g, w_in, conv_dw_w, conv_dw_b, conv_ln_g, conv_ln_b, swa_sinks, w_out,
                  norm_cross_g, w_cq, w_co, norm_ffn_g, peer_wq, peer_subkeys, peer_u, peer_v):
    b, t = h.shape[:2]
    xn = rmsnorm(h, norm_mix_g)
    proj = xn @ w_in
    c0 = 2 * D_CONV
    a = proj[..., :c0]
    q = partial_rope(proj[..., c0:c0 + D_ATTN].reshape(b, t, N_HEADS, HEAD_DIM), pos)
    k = partial_rope(proj[..., c0 + D_ATTN:c0 + D_ATTN + KV_DIM].reshape(b, t, N_KV_HEADS, HEAD_DIM), pos)
    v = proj[..., c0 + D_ATTN + KV_DIM:].reshape(b, t, N_KV_HEADS, HEAD_DIM)
    if conv_hist is None:
        conv_hist = jnp.zeros((b, CONV_WIDTH - 1, D_CONV), dtype=a.dtype)
    conv_out, new_conv = conformer_conv(a, conv_hist, conv_dw_w, conv_dw_b, conv_ln_g, conv_ln_b)
    if swa_k_hist is None:
        attn_out = swa_prompt(q, k, v, swa_sinks)
        new_k, new_v = k[:, -WINDOW:], v[:, -WINDOW:]
    else:
        k_all = jnp.concatenate([swa_k_hist.astype(k.dtype), k], axis=1)
        v_all = jnp.concatenate([swa_v_hist.astype(v.dtype), v], axis=1)
        attn_out = sink_gqa_attention(q, k_all, v_all, swa_sinks, None).reshape(b, t, D_ATTN)
        new_k, new_v = k_all[:, -WINDOW:], v_all[:, -WINDOW:]
    h = h + jnp.concatenate([conv_out, attn_out], axis=-1) @ w_out
    h = h + cross_attention(rmsnorm(h, norm_cross_g), mem_k, mem_v, w_cq, w_co)
    h = h + peer_ffn(rmsnorm(h, norm_ffn_g), peer_wq, peer_subkeys, peer_u, peer_v)
    return h, new_conv, new_k, new_v

def setup_inputs(seed: int = 0) -> dict:
    key = jax.random.key(seed)
    ks = jax.random.split(key, 32)

    def nrm(k, shape, scale):
        return jax.random.normal(k, shape, jnp.float32) * scale

    def gain(k, shape):
        return 1.0 + 0.01 * jax.random.normal(k, shape, jnp.float32)

    return {
        "x_prompt": nrm(ks[0], (BATCH, SEQ, D_MODEL), 1.0),
        "x_sample": nrm(ks[1], (DEC_BATCH, DEC_SEQ, D_MODEL), 1.0),
        "mem_prompt": nrm(ks[2], (BATCH, N_MEM, D_MODEL), 1.0),
        "cache_conv": nrm(ks[3], (DEPTH, DEC_BATCH, CONV_WIDTH - 1, D_CONV), 0.5),
        "cache_swa_k": nrm(ks[4], (DEPTH, DEC_BATCH, WINDOW, N_KV_HEADS, HEAD_DIM), 1.0),
        "cache_swa_v": nrm(ks[5], (DEPTH, DEC_BATCH, WINDOW, N_KV_HEADS, HEAD_DIM), 1.0),
        "cache_mem_k": nrm(ks[6], (DEPTH, DEC_BATCH, N_MEM, MEM_HEADS, MEM_HEAD_DIM), 1.0),
        "cache_mem_v": nrm(ks[7], (DEPTH, DEC_BATCH, N_MEM, MEM_HEADS, MEM_HEAD_DIM), 1.0),
        "norm_mix_g": gain(ks[8], (DEPTH, D_MODEL)),
        "w_in": nrm(ks[9], (DEPTH, D_MODEL, IN_COLS), D_MODEL ** -0.5),
        "conv_dw_w": nrm(ks[10], (DEPTH, CONV_WIDTH, D_CONV), CONV_WIDTH ** -0.5),
        "conv_dw_b": nrm(ks[11], (DEPTH, D_CONV), 0.01),
        "conv_ln_g": gain(ks[12], (DEPTH, D_CONV)),
        "conv_ln_b": nrm(ks[13], (DEPTH, D_CONV), 0.01),
        "swa_sinks": nrm(ks[14], (DEPTH, N_HEADS), 0.5),
        "w_out": nrm(ks[15], (DEPTH, D_MIX, D_MODEL), D_MIX ** -0.5),
        "norm_cross_g": gain(ks[16], (DEPTH, D_MODEL)),
        "norm_mem_g": gain(ks[17], (DEPTH, D_MODEL)),
        "w_cq": nrm(ks[18], (DEPTH, D_MODEL, D_MEM), D_MODEL ** -0.5),
        "w_ck": nrm(ks[19], (DEPTH, D_MODEL, D_MEM), D_MODEL ** -0.5),
        "w_cv": nrm(ks[20], (DEPTH, D_MODEL, D_MEM), D_MODEL ** -0.5),
        "w_co": nrm(ks[21], (DEPTH, D_MEM, D_MODEL), D_MEM ** -0.5),
        "norm_ffn_g": gain(ks[22], (DEPTH, D_MODEL)),
        "peer_wq": nrm(ks[23], (DEPTH, D_MODEL, PEER_HEADS * PEER_DK), D_MODEL ** -0.5),
        "peer_subkeys": nrm(ks[24], (DEPTH, PEER_HEADS, 2, N_KEYS, PEER_DK // 2), (PEER_DK // 2) ** -0.5),
        "peer_u": nrm(ks[25], (DEPTH, N_EXPERTS, D_MODEL), D_MODEL ** -0.5),
        "peer_v": nrm(ks[26], (DEPTH, N_EXPERTS, D_MODEL), PEER_HEADS ** -0.5),
        "norm_final_g": gain(ks[27], (D_MODEL,)),
    }

def reference(x_prompt, x_sample, mem_prompt, cache_conv, cache_swa_k, cache_swa_v, cache_mem_k, cache_mem_v,
              norm_mix_g, w_in, conv_dw_w, conv_dw_b, conv_ln_g, conv_ln_b, swa_sinks, w_out,
              norm_cross_g, norm_mem_g, w_cq, w_ck, w_cv, w_co,
              norm_ffn_g, peer_wq, peer_subkeys, peer_u, peer_v, norm_final_g):
    pos_p = jnp.arange(x_prompt.shape[1], dtype=jnp.int32)
    pos_s = PAST_LEN + jnp.arange(x_sample.shape[1], dtype=jnp.int32)
    hp, hs = x_prompt, x_sample
    conv_p, k_p, v_p, mk_p, mv_p = [], [], [], [], []
    conv_s, k_s, v_s = [], [], []
    for l in range(DEPTH):
        lw = (norm_mix_g[l], w_in[l], conv_dw_w[l], conv_dw_b[l], conv_ln_g[l], conv_ln_b[l], swa_sinks[l], w_out[l],
              norm_cross_g[l], w_cq[l], w_co[l], norm_ffn_g[l], peer_wq[l], peer_subkeys[l], peer_u[l], peer_v[l])
        mk, mv = memory_kv(mem_prompt, norm_mem_g[l], w_ck[l], w_cv[l])
        hp, c_new, k_new, v_new = layer_forward(hp, pos_p, None, None, None, mk, mv, *lw)
        conv_p.append(c_new)
        k_p.append(k_new)
        v_p.append(v_new)
        mk_p.append(mk)
        mv_p.append(mv)
        hs, c_new, k_new, v_new = layer_forward(hs, pos_s, cache_conv[l], cache_swa_k[l], cache_swa_v[l],
                                                cache_mem_k[l], cache_mem_v[l], *lw)
        conv_s.append(c_new)
        k_s.append(k_new)
        v_s.append(v_new)
    y_prompt = rmsnorm(hp, norm_final_g)
    y_sample = rmsnorm(hs, norm_final_g)
    return (y_prompt, y_sample, jnp.stack(conv_p), jnp.stack(k_p), jnp.stack(v_p), jnp.stack(mk_p), jnp.stack(mv_p),
            jnp.stack(conv_s), jnp.stack(k_s), jnp.stack(v_s))


_drawn_inputs = setup_inputs


def setup_inputs(seed=0):
    import zlib

    import numpy as np

    out = dict(_drawn_inputs(seed))
    spreads = {}
    factors = {'norm_mix_g': 4.559,
     'conv_dw_b': 3.139,
     'conv_ln_g': 4.309,
     'conv_ln_b': 4.744,
     'swa_sinks': 64.0,
     'norm_cross_g': 8.0,
     'norm_mem_g': 5.651,
     'norm_ffn_g': 18.333,
     'norm_final_g': 31.669}
    for name, (base, spread) in spreads.items():
        noise = np.random.default_rng([zlib.crc32(name.encode()), seed]).standard_normal(out[name].shape)
        drawn = base * np.exp(spread * noise) if base else spread * noise
        out[name] = jnp.asarray(drawn.astype(out[name].dtype))
    for name, factor in factors.items():
        out[name] = (out[name] * factor).astype(out[name].dtype)
    return out
```

```python
from contextlib import ExitStack, contextmanager

import concourse.bass as bass
import numpy as np
from concourse import mybir

F32 = mybir.dt.float32
F32R = mybir.dt.float32r
U32 = mybir.dt.uint32
ALU = mybir.AluOpType
ACT = mybir.ActivationFunctionType
AX = mybir.AxisListType
ds = bass.ds

P = 128
D = 2048
DT = D // P
NP_, NS = 256, 32
N = NP_ + NS
MEM = 256
CONV = 1024
CT = CONV // P
TAPS = 31
HIST = TAPS - 1
XW = HIST + NP_ + HIST + NS
YW = XW - HIST
S0 = HIST + NP_
HD = 64
CHUNK = 64
WINDOW = 128
PAST = 128
MH = 4
K16 = 16
NKEYS = 128
EPS = 1e-6
LOWEST = -3.0e38
ROT = 16
THETA = 500000.0

MEM0, GLU0, VKQ0, OUT0, CQ0, CO0, PQ0, U0, V0 = 0, 8, 24, 36, 52, 56, 60, 76, 204
SLOTS = V0 + 128
RAW = 4
U1_ITERS, U2_0, U2_ITERS = 12, 13, 9
TG = N // 16
BLK = 8
NBLK = 128 // BLK

C_ID, C_ONE, C_IOTA, C_ROT, C_COS, C_SIN = 0, 128, 256, 384, 512, 800
C_W = 1088
Q_GMIX, Q_GCROSS, Q_GMEM, Q_GFFN, Q_GFIN, Q_CW, Q_CB, Q_LG, Q_LB, Q_SINK = 0, 16, 32, 48, 64, 80, 328, 336, 344, 352
Q_W = 364


ROUTE_OPS = 27


class Own:

    def __init__(self, eng, sem):
        self.eng, self.sem, self.n, self.it = eng, sem, 0, 0

    def done(self, ins, by=1):
        ins.then_inc(self.sem, by)
        self.n += by

    def wait(self, back=0):
        self.eng.wait_ge(self.sem, self.it + self.n - back)

    @contextmanager
    def loop(self, i, start, end, per):
        n0 = self.n
        self.it = (i - start) * per
        yield
        assert self.n - n0 == per, (self.n - n0, per)
        self.n, self.it = n0 + per * (end - start), 0


def swa_units():
    units = []
    for g in range(4):
        lo, t0 = HD * (g % 2), 4 * (g // 2)
        for c in range(4):
            k0, k1 = max(0, c - 2) * CHUNK, (c + 1) * CHUNK
            first = 0 if k0 == 0 else 2
            pieces = [(a, min(P, k1 - k0 - a), first + a // P) for a in range(0, k1 - k0, P)]
            units.append(dict(kind="prompt", g=g, lo=lo, t0=t0, q0=c * CHUNK, nq=CHUNK, subs=2, rows=P,
                              keys=(k0, k1 - k0), nk=k1 - k0, pieces=pieces, sink=2 * g))
    for g in range(4):
        lo, t0 = HD * (g % 2), 4 * (g // 2)
        units.append(dict(kind="sample", g=g, lo=lo, t0=t0, q0=NP_, nq=NS, subs=1, rows=P, nk=WINDOW + NS,
                          pieces=[(0, P, 5), (P, NS, 4)], sink=8 + g))
    return units


def cross_units():
    units = []
    for t in range(3):
        for hp in range(2):
            units.append(dict(t=t, hp=hp, rows=P if t < 2 else NS, subs=2, nk=MEM, pieces=[(0, P, 0), (P, P, 1)]))
    return units


def build(nc, dr):
    swa, cross = swa_units(), cross_units()
    ctx = ExitStack()
    with ctx:
        def sb(where, name, shape, dt=F32):
            return where.enter_context(nc.sbuf_tensor(name, shape, dt))

        def sem(name):
            return ctx.enter_context(nc.semaphore(name))

        cst = sb(ctx, "cst", [P, C_W])
        par = sb(ctx, "par", [P, Q_W])
        negsink = sb(ctx, "negsink", [P, 12])
        eps = sb(ctx, "eps", [P, 1])
        hT = sb(ctx, "hT", [P, DT, N])
        xh, xl = sb(ctx, "xh", [P, DT, N], F32R), sb(ctx, "xl", [P, DT, N], F32R)
        raw = sb(ctx, "raw", [P, RAW, DT, P])
        wh, wl = sb(ctx, "wh", [P, 2, DT, P], F32R), sb(ctx, "wl", [P, 2, DT, P], F32R)
        root = sb(ctx, "root", [P, N])
        rstd = sb(ctx, "rstd", [P, 2, N])
        sqsum = sb(ctx, "sqsum", [P, N])
        sqt = sb(ctx, "sqt", [P, N])
        e = ExitStack()
        with e:
            mkvT = sb(e, "mkvT", [P, 8, MEM])
            mvtok = sb(e, "mvtok", [P, 2, MH * P])
            with ExitStack() as o:
                sqb = sb(o, "sqb", [P, 2, 2, N])
                gsb = sb(o, "gsb", [P, 3, N])
            smkT = sb(e, "smkT", [P, MH, MEM])
            smv = sb(e, "smv", [P, 2, MH * P])
            with ExitStack() as o:
                bh, bl = sb(o, "bh", [P, DT, N], F32R), sb(o, "bl", [P, DT, N], F32R)
            with ExitStack() as o:
                kvT = sb(o, "kvT", [P, 4, N])
                qch = sb(o, "qch", [P, NP_ // CHUNK, 8, CHUNK])
                qsm = sb(o, "qsm", [P, 8, NS])
                glu = sb(o, "glu", [P, CT, XW])
                y = sb(o, "y", [P, CT, N])
                cacc = sb(o, "cacc", [P, 2, YW])
            with ExitStack() as o:
                ch, cl = sb(o, "ch", [P, MH, N], F32R), sb(o, "cl", [P, MH, N], F32R)
            with ExitStack() as o:
                sb(o, "over_B", [P, 2 * DT * N])
                with ExitStack() as o1:
                    memT = sb(o1, "memT", [P, DT, MEM])
                with ExitStack() as o1:
                    prob = sb(o1, "prob", [P, 3, 512])
                    probT = sb(o1, "probT", [P, 4, P])
                    small = sb(o1, "small", [P, 2, 12])
                    with ExitStack() as o2:
                        ckT = sb(o2, "ckT", [P, 2, WINDOW])
                        vtok = sb(o2, "vtok", [P, 6, 256])
                        pacc = sb(o2, "pacc", [P, 2, YW])
                    with ExitStack() as o2:
                        qcT = sb(o2, "qcT", [P, MH, N])
        u = ExitStack()
        with u:
            with ExitStack() as o:
                ghl = sb(o, "ghl", [P, 2, N], F32R)
                ohL = sb(o, "ohL", [P, 2, 4, P], F32R)
            stok = sb(u, "stok", [P, 24, 2, NKEYS])
            with ExitStack() as o:
                gbuf = sb(o, "gbuf", [P, 2, P, 16])
            with ExitStack() as o:
                qp = sb(o, "qp", [P, 2, N])
                sb(o, "over_operand_C", [P, 2048 - 2 * N])
                skT = sb(o, "skT", [P, 16, NKEYS])
            sb(u, "over_gbuf", [P, 4096])
            ohA, ohB = sb(u, "ohA", [P, 2, 4, P], F32R), sb(u, "ohB", [P, 2, 4, P], F32R)
            gijT = sb(u, "gijT", [P, 3, N])
            tok32 = sb(u, "tok32", [P, 32])
            tv = sb(u, "tv", [P, 24, K16])
            gij = sb(u, "gij", [P, 3, 24, K16])
            den = sb(u, "den", [P, 24])
            v12 = sb(u, "v12", [P, 2, K16])
            i12 = sb(u, "i12", [P, 2, K16], U32)
            i12f = sb(u, "i12f", [P, 2, K16])
            sun = sb(u, "sun", [P, 2, NKEYS])
            top = sb(u, "top", [P, K16])
            cand = sb(u, "cand", [P, K16, K16])
            tsel = sb(u, "tsel", [P, K16], U32)
            tab = sb(u, "tab", [P, 2, K16], U32)
            eqb = sb(u, "eqb", [P, 2, K16, K16])
            hbg = sb(u, "hbg", [P, 8, N])
        v = ExitStack()
        with v:
            hin = sb(v, "hin", [P, BLK, N])
            gin = sb(v, "gin", [P, TG, BLK * 16])
            ah, al = sb(v, "ah", [P, 2, BLK, N], F32R), sb(v, "al", [P, 2, BLK, N], F32R)

        acc = ctx.enter_context(nc.psum_tensor("acc", [P, 4, 512], F32))
        mis = ctx.enter_context(nc.psum_tensor("mis", [P, 4, 512], F32))

        ident, ones, iota = cst[:, C_ID:C_ID + P], cst[:, C_ONE:C_ONE + P], cst[:, C_IOTA:C_IOTA + P]
        rotm = cst[:, C_ROT:C_ROT + P]
        cos, sin = cst[:, C_COS:C_COS + N], cst[:, C_SIN:C_SIN + N]
        sinks = par[:, Q_SINK:Q_SINK + 12]

        def bcast(ap, n, axis):
            return ap.unsqueeze(axis).broadcast_to([ap.shape[0]] + ([n] + list(ap.shape[1:]) if axis == 1 else list(ap.shape[1:]) + [n]))

        const_in, par_in = sem("const_in"), sem("par_in")
        mem_in = [sem(f"mem_in{n}") for n in range(4)]
        x_in = sem("x_in")
        raw_in = [sem(f"raw_in{n}") for n in range(RAW)]
        hi_done, lo_done, slot_used = sem("hi_done"), sem("lo_done"), sem("slot_used")
        acc_free = sem("acc_free")
        split_hi, split_lo = sem("split_hi"), sem("split_lo")
        sq_done, sq_used = sem("sq_done"), sem("sq_used")
        stat_done, root_done, rstd_done = sem("stat_done"), sem("root_done"), sem("rstd_done")
        pool_own, dve_own = sem("pool_own"), sem("dve_own")
        gate_done, sig_done, sgr_done = sem("gate_done"), sem("sig_done"), sem("sgr_done")
        hist_in, cache_in, conv_pool, conv_dve = sem("hist_in"), sem("cache_in"), sem("conv_pool"), sem("conv_dve")
        hist_zero, eps_ready, early_out, top_ready = sem("hist_zero"), sem("eps_ready"), sem("early_out"), sem("top_ready")
        vt_done, vt_out = sem("vt_done"), sem("vt_out")
        rot_done, rope_done = sem("rot_done"), sem("rope_done")
        ln_stat, ln_mean, ln_sq, ln_var, ln_root, ln_scaled, silu_done = (
            sem("ln_stat"), sem("ln_mean"), sem("ln_sq"), sem("ln_var"), sem("ln_root"), sem("ln_scaled"), sem("silu_done"))
        sinks_ready = sem("sinks_ready")

        def att_sems(tag):
            names = ("score", "negmax", "prob", "norm", "turned", "turnout", "value", "valhi", "vallo")
            return {n: sem(f"{tag}_{n}") for n in names}

        sw, cr = att_sems("swa"), att_sems("cross")
        co_done, co_free = sem("co_done"), sem("co_free")
        smem_in, sk_in = sem("smem_in"), sem("sk_in")
        stok_zero, pq_score, pq_out = sem("stok_zero"), sem("pq_score"), sem("pq_out")
        routed, exp_done, gate_w = sem("routed"), sem("exp_done"), sem("gate_w")
        gt_done, gt_out = sem("gt_done"), sem("gt_out")
        gelu_done, h_out = sem("gelu_done"), sem("h_out")
        oneA, oneB, g_done, g_evac = sem("oneA"), sem("oneB"), sem("g_done"), sem("g_evac")
        tok_in = sem("tok_in")
        g_out = [sem("g_out0"), sem("g_out1")]
        hg_in, prod_done, ah_done, act_ready = sem("hg_in"), sem("prod_done"), sem("ah_done"), sem("act_ready")
        fin_sq, fin_used, y_ready = sem("fin_sq"), sem("fin_used"), sem("y_ready")
        out_done = sem("out_done")

        def slot_no(base, i, s, stride=4):
            return base + stride * i + s

        def swa_scores(k, un):
            lo, t0, g = un["lo"], un["t0"], un["g"]
            rows = slice(lo, lo + HD)
            if un["kind"] == "prompt":
                k0, nk = un["keys"]
                return [(mis[:, k % 2, 256 * j:256 * j + nk],
                         qch[rows, un["q0"] // CHUNK, t0 + 2 * j:t0 + 2 * j + 2, :].rearrange("p t q -> p (t q)"),
                         kvT[rows, 2 + g // 2, k0:k0 + nk]) for j in range(2)]
            q = qsm[rows, t0:t0 + 4, :].rearrange("p t q -> p (t q)")
            return [(mis[:, k % 2, 0:WINDOW], q, ckT[rows, g // 2, :]),
                    (mis[:, k % 2, WINDOW:WINDOW + NS], q, kvT[rows, 2 + g // 2, NP_:N])]

        def swa_value(un, j, n):
            a, ln, tile = un["pieces"][n]
            return (mis[un["lo"]:un["lo"] + HD, 3, P * j:P * j + P], vtok[0:ln, tile, HD * un["g"]:HD * un["g"] + HD],
                    probT[0:ln, 2 * n + j, :])

        def swa_result(un):
            rows, t = slice(un["lo"], un["lo"] + HD), 8 + un["t0"]
            src = mis[rows, 3, 0:4 * un["nq"]].rearrange("p (t q) -> p t q", t=4)
            at = (rows, slice(t, t + 4), slice(un["q0"], un["q0"] + un["nq"]))
            return xh[at], xl[at], src

        def cross_scores(k, un):
            R, c0 = un["rows"], un["t"] * P
            keys = smkT if un["t"] == 2 else mkvT
            return [(mis[0:R, k % 2, 256 * j:256 * j + MEM], qcT[:, 2 * un["hp"] + j, c0:c0 + R],
                     keys[:, 2 * un["hp"] + j, :]) for j in range(2)]

        def cross_value(un, j, n):
            head, R = 2 * un["hp"] + j, un["rows"]
            vals = smv if un["t"] == 2 else mvtok
            return mis[:, 3, P * j:P * j + R], vals[:, n, P * head:P * head + P], probT[:, 2 * n + j, 0:R]

        def cross_result(un):
            R, c0, h0 = un["rows"], un["t"] * P, 2 * un["hp"]
            at = (slice(0, P), slice(h0, h0 + 2), slice(c0, c0 + R))
            return ch[at], cl[at], mis[:, 3, 0:2 * P].rearrange("p (j r) -> p j r", j=2)[:, :, 0:R]

        SWA = dict(units=swa, sems=sw, scores=swa_scores, value=swa_value, result=swa_result, scale=HD ** -0.5)
        CROSS = dict(units=cross, sems=cr, scores=cross_scores, value=cross_value, result=cross_result, scale=P ** -0.5)

        block = ctx.enter_context(nc.Block())

        @block.sync
        def _(sp):
            sp.dma_start(par[:], dr["par"]).then_inc(par_in, 16)
            sp.dma_start(raw[:, 0], dr["w_mem"][0]).then_inc(raw_in[0], 16)
            for n in range(4):
                sp.dma_start(memT[:, 4 * n:4 * n + 4, :], dr["memT"][:, 4 * n:4 * n + 4, :]).then_inc(mem_in[n], 16)
            sp.dma_start(raw[:, 1], dr["w_mem"][1]).then_inc(raw_in[1], 16)
            sp.dma_start(cst[:], dr["cst"]).then_inc(const_in, 16)
            sp.dma_start(hT[:], dr["xT"]).then_inc(x_in, 16)
            for s in range(2, RAW):
                sp.dma_start(raw[:, s], dr["w_mem"][s]).then_inc(raw_in[s], 16)

            def stream(name, base, start, n_iters):
                with sp.Fori(start, n_iters) as i:
                    for s in range(4):
                        sp.wait_ge(lo_done, slot_no(base, i, s) - RAW + 1)
                        sp.dma_start(raw[:, s], dr[name][4 * i + s]).then_inc(raw_in[s], 16)

            stream("w_mem", MEM0, 1, 2)
            stream("w_mix", GLU0, 0, 7)
            stream("w_out", OUT0, 0, 4)
            stream("w_cq", CQ0, 0, 1)
            stream("w_co", CO0, 0, 1)
            stream("w_pq", PQ0, 0, 4)
            stream("u", U0, 0, 32)
            sp.wait_ge(h_out, 32)
            for b in range(2):
                sp.wait_ge(g_out[b], 16 * U2_ITERS)
            sp.wait_ge(routed, 1)

            def load_hg(b):
                for a in range(2):
                    sp.dma_start(hin[:, 4 * a:4 * a + 4, :], dr["h"][2 * b + a]).then_inc(hg_in, 16)
                sp.dma_start(gin[:], dr["G"][b]).then_inc(hg_in, 16)

            load_hg(0)

            def v_iteration(i, last):
                for s in range(16):
                    b = 2 * i + s // 8
                    sp.wait_ge(lo_done, slot_no(V0, i, s, 16) - RAW + 1)
                    sp.dma_start(raw[:, s % 4], dr["v"][16 * i + s]).then_inc(raw_in[s % 4], 16)
                    if s % 8 == 1 and not (last and s > 8):
                        sp.wait_ge(act_ready, b + 1)
                        if s > 8:
                            sp.wait_ge(h_out, 16 * 32)
                        load_hg(b + 1)

            with sp.Fori(0, NBLK // 2 - 1) as i:
                v_iteration(i, False)
            v_iteration(NBLK // 2 - 1, True)
            for n in range(4):
                sp.wait_ge(y_ready, 4 * n + 4)
                sp.dma_start(dr["yT"][:, 4 * n:4 * n + 4, :], hT[:, 4 * n:4 * n + 4, :]).then_inc(out_done, 16)
            sp.wait_ge(early_out, 16 * 7)
            sp.wait_ge(out_done, 16 * 4)

        @block.scalar
        def _(act):
            def hi_next(base, i, s, stride=4):
                n = s + 1
                act.wait_ge(raw_in[n % 4], 16 * (base // 4 + (stride // 4) * i + n // 4 + 1))
                if not (isinstance(i, int) and slot_no(base, i, s, stride) == 0):
                    act.wait_ge(slot_used, slot_no(base, i, s, stride))
                act.activation(wh[:, n % 2], raw[:, n % 4], ACT.Copy).then_inc(hi_done, 1)

            def split(dst, src, gain):
                act.activation(dst, src, ACT.Copy, scale=gain).then_inc(split_hi, 1)

            def one(ap):
                return ap.rearrange("p a n -> p (a n)")

            def norm_root(n, bank, which, count, cols=N):
                act.wait_ge(which, count)
                if n:
                    act.wait_ge(rstd_done, n)
                act.activation(root[:, 0:cols], mis[:, bank, 0:cols], ACT.Sqrt, bias=eps[:, 0:1], scale=1.0 / D).then_inc(root_done, 1)

            act.wait_ge(raw_in[0], 16)
            act.activation(wh[:, 0], raw[:, 0], ACT.Copy).then_inc(hi_done, 1)
            act.wait_ge(par_in, 16)
            for t in range(DT):
                if t % 4 == 0:
                    act.wait_ge(mem_in[t // 4], 16)
                split(bh[:, t, 0:MEM], memT[:, t, :], par[:, Q_GMEM + t:Q_GMEM + t + 1])
            for g in range(8):
                hi_next(MEM0, g // 4, g % 4)
                if g == 0:
                    act.wait_ge(x_in, 16)
                for t in (2 * g, 2 * g + 1):
                    split(xh[:, t, :], hT[:, t, :], par[:, Q_GMIX + t:Q_GMIX + t + 1])
                if g == 0:
                    act.wait_ge(eps_ready, 1)
                    norm_root(0, 3, sq_used, 8, MEM)
                if g == 5:
                    norm_root(1, 2, sq_used, 16)
            with act.Fori(0, 4) as i:
                for s in range(4):
                    hi_next(GLU0, i, s)
                    if s % 2 == 0:
                        act.wait_ge(gate_done, 2 * i + s // 2 + 1)
                        act.activation(gsb[:, 1, :], gsb[:, 0, :], ACT.Sigmoid).then_inc(sig_done, 1)
            with act.Fori(0, 3) as i:
                for s in range(4):
                    hi_next(VKQ0, i, s)
            for h in range(2):
                act.wait_ge(vt_done, h + 1)
                act.activation(mvtok[:, :, 2 * P * h:2 * P * h + 2 * P], mis[:, h, :].rearrange("p (m c) -> p m c", m=2),
                               ACT.Copy).then_inc(vt_out, 1)
            for n, (bank, ln, tiles) in enumerate(((0, P, (0, 2)), (1, P, (2, 3)), (2, CHUNK, (3, 4)), (3, NS, (4, 5)))):
                act.wait_ge(vt_done, 3 + n)
                nt = tiles[1] - tiles[0]
                act.activation(vtok[0:ln, tiles[0]:tiles[1], :],
                               mis[0:ln, bank, 0:256 * nt].rearrange("p (t c) -> p t c", t=nt), ACT.Copy).then_inc(vt_out, 1)

            def attention(A, hooks):
                S, units, n = A["sems"], A["units"], len(A["units"])
                for k in range(n + 4):
                    if k in hooks:
                        hooks[k]()
                    if 0 <= k - 3 < n:
                        un = units[k - 3]
                        act.wait_ge(S["turned"], k - 2)
                        if k >= 4:
                            act.wait_ge(S["value"], k - 3)
                        R = un["rows"]
                        for m, (a, ln, _) in enumerate(un["pieces"]):
                            last = act.activation(probT[0:ln, 2 * m:2 * m + un["subs"], 0:R],
                                                  mis[0:ln, 2, 256 * m:256 * m + P * un["subs"]].rearrange("p (j r) -> p j r", r=P)[:, :, 0:R], ACT.Copy)
                        last.then_inc(S["turnout"], 1)
                    if 0 <= k - 4 < n:
                        act.wait_ge(S["value"], k - 3)
                        dh, _, src = A["result"](units[k - 4])
                        act.activation(dh, src, ACT.Copy).then_inc(S["valhi"], 1)
                    if k < n:
                        un, r = units[k], k % 2
                        R = un["rows"]
                        act.wait_ge(S["negmax"], k + 1)
                        if k >= 3:
                            act.wait_ge(S["turned"], k - 2)
                        for j in range(un["subs"]):
                            last = act.activation(prob[0:R, k % 3, 256 * j:256 * j + un["nk"]], mis[0:R, r, 256 * j:256 * j + un["nk"]], ACT.Exp,
                                                  bias=small[0:R, r, 2 + j:3 + j], scale=A["scale"], accum_out=small[0:R, r, 6 + j:7 + j])
                        if A is SWA:
                            last = act.activation(small[:, r, 8:8 + un["subs"]], small[:, r, 4:4 + un["subs"]], ACT.Exp)
                        last.then_inc(S["prob"], 1)

            def ln_squares():
                act.wait_ge(ln_mean, 2)
                for c in range(4):
                    if c >= 2:
                        act.wait_ge(ln_var, c - 1)
                    act.activation(sqb[:, c % 2], y[:, 2 * c:2 * c + 2, :], ACT.Square).then_inc(ln_sq, 1)

            def ln_rootf():
                act.wait_ge(ln_var, 4)
                act.activation(root[:], acc[:, 1, 0:N], ACT.Sqrt, bias=eps[:, 0:1], scale=1.0 / CONV).then_inc(ln_root, 1)

            def conv_silu():
                act.wait_ge(ln_scaled, 1)
                for t in range(CT):
                    act.activation(y[:, t, :], y[:, t, :], ACT.Silu, bias=par[:, Q_LB + t:Q_LB + t + 1],
                                   scale=par[:, Q_LG + t:Q_LG + t + 1]).then_inc(silu_done, 1)
                for t in range(CT):
                    act.wait_ge(silu_done, t + 1)
                    act.activation(xh[:, t, :], y[:, t, :], ACT.Copy).then_inc(split_hi, 1)

            attention(SWA, {12: ln_squares, 14: ln_rootf, 17: conv_silu})
            act.wait_ge(split_lo, 2 * DT + CT)
            act.wait_ge(early_out, 16 * 7)
            with act.Fori(0, 4) as i:
                for s in range(4):
                    hi_next(OUT0, i, s)
                    act.wait_ge(acc_free, slot_no(OUT0, i, s) + 5)
                    split(one(bh[:, ds(4 * i + s, 1), :]), one(hT[:, ds(4 * i + s, 1), :]), par[:, ds(Q_GCROSS + 4 * i + s, 1)])
            for s in range(4):
                hi_next(CQ0, 0, s)
                if s == 0:
                    norm_root(2, 3, stat_done, 1)
            attention(CROSS, {})
            for s in range(4):
                hi_next(CO0, 0, s)
                for m in range(4 * s, 4 * s + 4):
                    act.wait_ge(co_free, m + 1)
                    split(xh[:, m, :], hT[:, m, :], par[:, Q_GFFN + m:Q_GFFN + m + 1])
            def pq(i, first):
                for s in range(4):
                    hi_next(PQ0, i, s)
                    if first and s == 0:
                        norm_root(3, 2, stat_done, 2)
                    if s > 0:
                        pq_scores(i, s - 1)
                pq_scores(i, 3)

            def pq_scores(i, s):
                act.wait_ge(pq_score, 4 * i + s + 1)
                h = 2 * i + s // 2
                src = mis[:, s % 2, 0:3 * P].rearrange("p (t c) -> p t c", t=3)
                view = stok[:].rearrange("p (t h) j c -> p t h j c", t=3)[:, :, ds(h, 1), s % 2, :]
                act.activation(view[:, 0:2].rearrange("p t a c -> p (t a) c"), src[:, 0:2, :], ACT.Copy)
                act.activation(view[0:NS, 2:3].rearrange("p t a c -> p (t a) c"), src[0:NS, 2:3, :], ACT.Copy).then_inc(pq_out, 1)

            act.wait_ge(stok_zero, 1)
            pq(0, True)
            with act.Fori(1, 4) as i:
                pq(i, False)

            def gelu_of(it_before):
                act.wait_ge(acc_free, U0 + 4 * it_before + 8)
                act.activation(hbg[:, 4:8, :], hbg[:, 0:4, :], ACT.Gelu).then_inc(gelu_done, 1)
                act.wait_ge(gelu_done, it_before + 2)
                act.dma_start(dr["h"][it_before], hbg[:, 4:8, :]).then_inc(h_out, 16)

            def u_iteration(it, gelu=True, g_iter=None, g_first=False, hook=None):
                for s in range(4):
                    hi_next(U0, it, s)
                    if s == 0 and gelu:
                        if not (isinstance(it, int) and it == 1):
                            act.wait_ge(h_out, 16 * (it - 1))
                        gelu_of(it - 1)
                    if g_iter is not None:
                        if s == 0 and not g_first:
                            g_out_of(g_iter - 1, 3, True)
                            g_store(g_iter - 1, 1)
                        if s > 0:
                            g_out_of(g_iter, s - 1, g_first)
                        if s == 2:
                            g_store(g_iter, 0)
                    if hook:
                        hook(s)

            def g_out_of(gi, s, first):
                half = s // 2
                if not first and s % 2 == 0:
                    act.wait_ge(g_out[half], 16 * gi)
                for b in range(2):
                    n = 2 * s + b
                    act.wait_ge(g_done, 8 * gi + n + 3)
                    k = 4 * (n % 4)
                    act.activation(gbuf[:, half, :, k:k + 4], mis[:, b, :].rearrange("p (t j) -> p j t", t=4), ACT.Copy).then_inc(g_evac, 1)

            def g_store(gi, half):
                act.wait_ge(g_evac, 8 * gi + 4 * half + 6)
                dst = dr["G"][:, :, ds(2 * gi + half, 1), :].rearrange("b p a f -> p b (a f)")
                act.dma_start(dst, gbuf[:, half].rearrange("p (b j) t -> p b (j t)", b=NBLK)).then_inc(g_out[half], 16)

            act.sem_inc(gelu_done, 1)
            act.sem_inc(g_evac, 2)
            u_iteration(0, gelu=False)
            u_iteration(1)
            with act.Fori(2, U1_ITERS) as i:
                u_iteration(i)

            def softmax_exp(s):
                if s == 0:
                    act.wait_ge(top_ready, 1)
                    act.activation(tv[:], tv[:], ACT.Exp).then_inc(exp_done, 1)

            u_iteration(U1_ITERS, hook=softmax_exp)
            for n in range(3):
                act.wait_ge(gt_done, n + 1)
                act.activation(gijT[:, n, :], mis[:, n, 0:N], ACT.Copy).then_inc(gt_out, 1)
            act.activation(ghl[:, 0, :], mis[:, 0, 0:N], ACT.Copy).then_inc(gt_out, 1)
            u_iteration(U2_0, g_iter=0, g_first=True)
            with act.Fori(1, U2_ITERS) as i:
                u_iteration(i + U2_0, g_iter=i)
            g_out_of(U2_ITERS - 1, 3, True)
            g_store(U2_ITERS - 1, 1)
            with act.Fori(U2_0 + U2_ITERS, 31) as i:
                u_iteration(i)

            def act_hi(b, r):
                act.wait_ge(prod_done, b + 1)
                act.activation(ah[:, r], hin[:], ACT.Copy).then_inc(ah_done, 1)

            u_iteration(31, hook=lambda s: act_hi(0, 0) if s == 1 else None)
            act.wait_ge(h_out, 16 * 31)
            gelu_of(31)

            def v_iteration(i, last):
                for s in range(16):
                    if not (last and s == 15):
                        hi_next(V0, i, s, 16)
                    if s % 8 == 3 and not (last and s > 8):
                        act_hi(2 * i + s // 8 + 1, (s // 8 + 1) % 2)

            with act.Fori(0, NBLK // 2 - 1) as i:
                v_iteration(i, False)
            v_iteration(NBLK // 2 - 1, True)
            for n in range(4):
                act.wait_ge(acc_free, SLOTS + 4)
                if n >= 2:
                    act.wait_ge(fin_used, n - 1)
                act.activation(hin[:, 4 * (n % 2):4 * (n % 2) + 4, :], hT[:, 4 * n:4 * n + 4, :], ACT.Square).then_inc(fin_sq, 1)
            norm_root(4, 3, stat_done, 3)

        @block.vector
        def _(dve):
            own = Own(dve, dve_own)

            def lo_next(base, i, s, stride=4):
                n = s + 1
                dve.wait_ge(hi_done, slot_no(base, i, s, stride) + 2)
                dve.tensor_tensor(wl[:, n % 2], raw[:, n % 4], wh[:, n % 2].bitcast(F32), ALU.subtract).then_inc(lo_done, 1)

            def slot_ready(base, i, s, stride=4):
                dve.wait_ge(slot_used, slot_no(base, i, s, stride) + 1)

            def split(dst, src, gain, hi, count):
                dve.wait_ge(split_hi, count)
                dve.scalar_tensor_tensor(dst, src, gain, hi.bitcast(F32), ALU.mult, ALU.subtract).then_inc(split_lo, 1)

            def one(ap):
                return ap.rearrange("p a n -> p (a n)")

            def norm_recip(n, bank, cols=N):
                r, t = rstd[:, n % 2, 0:cols], root[:, 0:cols]
                dve.wait_ge(root_done, n + 1)
                own.done(dve.reciprocal(r, t))
                own.wait(0)
                own.done(dve.tensor_scalar(t, mis[:, bank, 0:cols], 1.0 / D, EPS, ALU.mult, ALU.add))
                for _ in range(2):
                    own.wait(0)
                    own.done(dve.tensor_tensor(t, t, r, ALU.mult))
                own.wait(0)
                own.done(dve.tensor_scalar(t, t, -0.5, 1.5, ALU.mult, ALU.add))
                own.wait(0)
                dve.tensor_tensor(r, r, t, ALU.mult).then_inc(rstd_done, 1)
                dve.wait_ge(rstd_done, n + 1)

            dve.sem_inc(acc_free, 4)
            dve.memset(eps[:], EPS).then_inc(eps_ready, 1)
            dve.wait_ge(hi_done, 1)
            dve.tensor_tensor(wl[:, 0], raw[:, 0], wh[:, 0].bitcast(F32), ALU.subtract).then_inc(lo_done, 1)
            dve.wait_ge(par_in, 16)
            dve.tensor_scalar(negsink[:], sinks, -1.0, None, ALU.mult).then_inc(sinks_ready, 1)
            for t in range(DT):
                split(bl[:, t, 0:MEM], memT[:, t, :], par[:, Q_GMEM + t:Q_GMEM + t + 1], bh[:, t, 0:MEM], t + 1)
            for g in range(8):
                lo_next(MEM0, g // 4, g % 4)
                for t in (2 * g, 2 * g + 1):
                    split(xl[:, t, :], hT[:, t, :], par[:, Q_GMIX + t:Q_GMIX + t + 1], xh[:, t, :], DT + t + 1)
                if g == 0:
                    norm_recip(0, 3, MEM)
                slot_ready(MEM0, 0, g)
                dve.tensor_tensor(mkvT[:, g, :], acc[:, g % 4, 0:MEM], rstd[:, 0, 0:MEM], ALU.mult).then_inc(acc_free, 1)
                if g == 5:
                    norm_recip(1, 2)

            def conv(ct, first, q):
                for n in range(8 * q, 8 * q + 8):
                    a = n % 2
                    if n == 31:
                        own.wait(0)
                        dve.tensor_tensor(one(y[:, ds(ct, 1), 0:NP_]), cacc[:, 0, 0:NP_], cacc[:, 1, 0:NP_], ALU.add)
                        dve.tensor_tensor(one(y[:, ds(ct, 1), NP_:N]), cacc[:, 0, S0:YW], cacc[:, 1, S0:YW], ALU.add).then_inc(conv_dve, 1)
                        continue
                    x = one(glu[:, ds(ct, 1), n:n + YW])
                    w = par[:, ds(Q_CW + TAPS * ct + n, 1)]
                    if n >= 2:
                        own.wait(1)
                    elif not first:
                        dve.wait_ge(conv_dve, ct)
                    if n == 0:
                        own.done(dve.tensor_scalar(cacc[:, 0, :], x, w, par[:, ds(Q_CB + ct, 1)], ALU.mult, ALU.add))
                    elif n == 1:
                        own.done(dve.tensor_scalar(cacc[:, 1, :], x, w, None, ALU.mult))
                    else:
                        own.done(dve.scalar_tensor_tensor(cacc[:, a, :], x, w, cacc[:, a, :], ALU.mult, ALU.add))

            def glu_iteration(i, with_conv, first=False):
                for s in range(4):
                    lo_next(GLU0, i, s)
                    slot_ready(GLU0, i, s)
                    if s % 2 == 0:
                        if not (first and s == 0):
                            dve.wait_ge(sig_done, 2 * i + s // 2)
                        dve.tensor_tensor(gsb[:, 0, :], acc[:, s, 0:N], rstd[:, 1, :], ALU.mult).then_inc(gate_done, 1)
                        dve.wait_ge(gate_done, 2 * i + s // 2 + 1)
                        dve.sem_inc(acc_free, 1)
                    else:
                        dve.wait_ge(sgr_done, 2 * i + s // 2 + 1)
                        ct = 2 * i + s // 2
                        dve.tensor_tensor(one(glu[:, ds(ct, 1), HIST:HIST + NP_]), acc[:, s, 0:NP_], gsb[:, 2, 0:NP_], ALU.mult)
                        dve.tensor_tensor(one(glu[:, ds(ct, 1), HIST + S0:XW]), acc[:, s, NP_:N], gsb[:, 2, NP_:N], ALU.mult).then_inc(acc_free, 1)
                    if with_conv:
                        conv(i - 1, isinstance(i, int) and i == 1, s)

            dve.wait_ge(const_in, 16)
            glu_iteration(0, False, first=True)
            dve.wait_ge(acc_free, GLU0 + 8)
            dve.wait_ge(hist_zero, 1)
            dve.wait_ge(hist_in, 16)
            glu_iteration(1, True)
            with dve.Fori(2, 4) as i, own.loop(i, 2, 4, 31):
                dve.wait_ge(acc_free, GLU0 + 4 + 4 * i)
                glu_iteration(i, True)
            dve.wait_ge(acc_free, VKQ0 + 4)

            def vkq_iteration(i, first):
                for s in range(4):
                    lo_next(VKQ0, i, s)
                    slot_ready(VKQ0, i, s)
                    if first:
                        dve.tensor_tensor(kvT[:, s, :], acc[:, s, 0:N], rstd[:, 1, :], ALU.mult).then_inc(acc_free, 1)
                    else:
                        t = 4 * (i - 1) + s
                        for dst, src, r in q_parts(t, acc[:, s, 0:N], rstd[:, 1, :]):
                            ins = dve.tensor_tensor(dst, src, r, ALU.mult)
                        ins.then_inc(acc_free, 1)
                    conv(i + 3, False, s)

            def q_parts(t, *others):
                yield [qch[:, :, ds(t, 1), :].rearrange("p c a q -> p (c a) q")] + [
                    o[:, 0:NP_].rearrange("p (c q) -> p c q", q=CHUNK) for o in others]
                yield [one(qsm[:, ds(t, 1), :])] + [o[:, NP_:N] for o in others]

            vkq_iteration(0, True)
            with dve.Fori(1, 3) as i, own.loop(i, 1, 3, 31):
                vkq_iteration(i, False)
            for j in range(10):
                ops = [mis[:, j % 2, 0:N], sin, cos, cacc[:, 0, 0:N]]
                parts = [[kvT[:, 2 + j, :]] + ops] if j < 2 else list(q_parts(j - 2, *ops))
                dve.wait_ge(rot_done, j + 1)
                if j:
                    dve.wait_ge(rope_done, j)
                else:
                    dve.wait_ge(conv_dve, 6)
                for x, other, sn, cs, tmp in parts:
                    own.done(dve.tensor_tensor(tmp, other, sn, ALU.mult))
                    own.done(dve.tensor_tensor(x, x, cs, ALU.mult))
                own.wait(0)
                for x, other, sn, cs, tmp in parts:
                    ins = dve.tensor_tensor(x, x, tmp, ALU.add)
                ins.then_inc(rope_done, 1)

            def attention(A, hooks):
                S, units, n = A["sems"], A["units"], len(A["units"])
                for k in range(n + 4):
                    if k in hooks:
                        hooks[k]()
                    if 0 <= k - 4 < n:
                        dve.wait_ge(S["valhi"], k - 3)
                        dh, dl, src = A["result"](units[k - 4])
                        dve.tensor_tensor(dl, src, dh.bitcast(F32), ALU.subtract).then_inc(S["vallo"], 1)
                    if k < n:
                        un, r = units[k], k % 2
                        R, m = un["rows"], un["subs"]
                        dve.wait_ge(S["score"], k + 1)
                        if k >= 2:
                            dve.wait_ge(S["prob"], k - 1)
                            dve.wait_ge(S["norm"], k - 1)
                        src = mis[0:R, r, :].rearrange("p (j c) -> p j c", j=2)[:, 0:m, 0:un["nk"]]
                        own.done(dve.tensor_reduce(small[0:R, r, 0:m], src, AX.X, ALU.max))
                        own.wait(0)
                        if A is SWA:
                            c = un["sink"]
                            own.done(dve.scalar_tensor_tensor(small[:, r, 2:2 + m], small[:, r, 0:m], -A["scale"], negsink[:, c:c + m], ALU.mult, ALU.min))
                            own.wait(0)
                            dve.tensor_tensor(small[:, r, 4:4 + m], small[:, r, 2:2 + m], sinks[:, c:c + m], ALU.add).then_inc(S["negmax"], 1)
                        else:
                            dve.tensor_scalar(small[0:R, r, 2:2 + m], small[0:R, r, 0:m], -A["scale"], None, ALU.mult).then_inc(S["negmax"], 1)
                    if 0 <= k - 1 < n:
                        un, r = units[k - 1], (k - 1) % 2
                        R, m = un["rows"], un["subs"]
                        dve.wait_ge(S["prob"], k)
                        tot = small[0:R, r, 6:6 + m]
                        if A is SWA:
                            own.done(dve.tensor_tensor(tot, tot, small[0:R, r, 8:8 + m], ALU.add))
                            own.wait(0)
                        own.done(dve.reciprocal(small[0:R, r, 10:10 + m], tot))
                        own.wait(0)
                        for j in range(m):
                            p = prob[0:R, (k - 1) % 3, 256 * j:256 * j + un["nk"]]
                            last = dve.tensor_scalar(p, p, small[0:R, r, 10 + j:11 + j], None, ALU.mult)
                        last.then_inc(S["norm"], 1)

            def ln_center():
                dve.wait_ge(ln_stat, 1)
                dve.tensor_scalar(sqt[:], acc[:, 0, 0:N], 1.0 / CONV, None, ALU.mult).then_inc(ln_mean, 1)
                dve.wait_ge(ln_mean, 1)
                dve.tensor_tensor(y[:], y[:], bcast(sqt[:], CT, 1), ALU.subtract).then_inc(ln_mean, 1)

            def ln_scale():
                dve.wait_ge(ln_root, 1)
                own.done(dve.reciprocal(sqsum[:], root[:]))
                own.wait(0)
                dve.wait_ge(ln_sq, 4)
                dve.tensor_tensor(y[:], y[:], bcast(sqsum[:], CT, 1), ALU.mult).then_inc(ln_scaled, 1)

            def conv_lo():
                for t in range(CT):
                    dve.wait_ge(split_hi, 2 * DT + t + 1)
                    dve.tensor_tensor(xl[:, t, :], y[:, t, :], xh[:, t, :].bitcast(F32), ALU.subtract).then_inc(split_lo, 1)

            dve.wait_ge(rope_done, 10)
            conv_quarters = {2 * q: lambda q=q: conv(CT - 2, False, q) for q in range(4)}
            attention(SWA, {**conv_quarters, 10: ln_center, 15: ln_scale, 19: conv_lo})
            with dve.Fori(0, 4) as i:
                for s in range(4):
                    lo_next(OUT0, i, s)
                    slot_ready(OUT0, i, s)
                    t = one(hT[:, ds(4 * i + s, 1), :])
                    dve.tensor_tensor(t, t, acc[:, s, 0:N], ALU.add).then_inc(acc_free, 1)
                    dve.wait_ge(acc_free, slot_no(OUT0, i, s) + 5)
                    split(one(bl[:, ds(4 * i + s, 1), :]), t, par[:, ds(Q_GCROSS + 4 * i + s, 1)],
                          one(bh[:, ds(4 * i + s, 1), :]), 2 * DT + CT + 4 * i + s + 1)
            for s in range(4):
                lo_next(CQ0, 0, s)
                if s == 0:
                    norm_recip(2, 3)
                slot_ready(CQ0, 0, s)
                dve.tensor_tensor(qcT[:, s, :], acc[:, s, 0:N], rstd[:, 0, :], ALU.mult).then_inc(acc_free, 1)
            attention(CROSS, {})
            for s in range(4):
                lo_next(CO0, 0, s)
                for m in range(4 * s, 4 * s + 4):
                    if m % 4 < 3:
                        dve.wait_ge(co_done, 3 * s + m % 4 + 1)
                    else:
                        slot_ready(CO0, 0, s)
                    dve.tensor_tensor(hT[:, m, :], hT[:, m, :], acc[:, m % 4, 0:N], ALU.add).then_inc(co_free, 1)
                    dve.wait_ge(co_free, m + 1)
                    split(xl[:, m, :], hT[:, m, :], par[:, Q_GFFN + m:Q_GFFN + m + 1], xh[:, m, :], 3 * DT + CT + m + 1)
                dve.wait_ge(co_free, 4 * s + 4)
                dve.sem_inc(acc_free, 1)

            def pq(i, first):
                for s in range(4):
                    lo_next(PQ0, i, s)
                    if first and s == 0:
                        norm_recip(3, 2)
                    slot_ready(PQ0, i, s)
                    if not (first and s < 2):
                        dve.wait_ge(pq_score, 4 * i + s - 1)
                    dve.tensor_tensor(qp[:, s % 2, :], acc[:, s, 0:N], rstd[:, 1, :], ALU.mult).then_inc(acc_free, 1)

            pq(0, True)
            with dve.Fori(1, 4) as i:
                pq(i, False)

            iota16 = iota[:, 0:K16]

            def waited(back):
                own.wait(back)
                dve.nop(nofuse=True)

            def route(un, part):
                S = [sun[:, j, :] for j in range(2)]
                if part == 0:
                    waited(0)
                    own.done(dve.tensor_copy(sun[:], stok[:, ds(un, 1), :, :].rearrange("p a j c -> p (a j) c")))
                    waited(0)
                    for lo_ in (0, 8):
                        for j in range(2):
                            own.done(dve.max(v12[:, j, lo_:lo_ + 8], S[j]))
                        for j in range(2):
                            waited(1)
                            own.done(dve.max_index(i12[:, j, lo_:lo_ + 8], v12[:, j, lo_:lo_ + 8], S[j]))
                        if lo_ == 0:
                            for j in range(2):
                                waited(1)
                                own.done(dve.match_replace(S[j], v12[:, j, 0:8], S[j], LOWEST))
                            waited(0)
                    waited(0)
                    own.done(dve.tensor_copy(i12f[:], i12[:]))
                    own.done(dve.tensor_tensor(cand[:], bcast(v12[:, 0, :], K16, 2), bcast(v12[:, 1, :], K16, 1), ALU.add))
                    return
                flat = cand[:].rearrange("p a b -> p (a b)")
                waited(0)
                for lo_ in (0, 8):
                    own.done(dve.max(top[:, lo_:lo_ + 8], flat))
                    waited(0)
                    own.done(dve.max_index(tsel[:, lo_:lo_ + 8], top[:, lo_:lo_ + 8], flat))
                    waited(0)
                    if lo_ == 0:
                        own.done(dve.match_replace(flat, top[:, 0:8], flat, LOWEST))
                        waited(0)
                own.done(dve.tensor_copy(one(tv[:, ds(un, 1), :]), top[:]))
                own.done(dve.tensor_scalar(tab[:, 0, :], tsel[:], 4, None, ALU.logical_shift_right))
                own.done(dve.tensor_scalar(tab[:, 1, :], tsel[:], 15, None, ALU.bitwise_and))
                for j in range(2):
                    waited(1)
                    own.done(dve.tensor_tensor(eqb[:, j], bcast(tab[:, j, :], K16, 2), bcast(iota16, K16, 1), ALU.is_equal))
                for j in range(2):
                    waited(1)
                    own.done(dve.tensor_tensor(eqb[:, j], eqb[:, j], bcast(i12f[:, j, :], K16, 1), ALU.mult))
                for j in range(2):
                    waited(1)
                    own.done(dve.tensor_reduce(gij[:, 1 + j, ds(un, 1), :].rearrange("p a c -> p (a c)"), eqb[:, j], AX.X, ALU.add))

            def u_evac(it, s):
                slot_ready(U0, it, s)
                if s == 0:
                    dve.wait_ge(gelu_done, it + 1)
                dve.tensor_tensor(hbg[:, s, :], acc[:, s, 0:N], rstd[:, 1, :], ALU.mult).then_inc(acc_free, 1)

            dve.wait_ge(pq_out, 16)
            with dve.Fori(0, U1_ITERS) as i, own.loop(i, 0, U1_ITERS, ROUTE_OPS * 2):
                for s in range(4):
                    lo_next(U0, i, s)
                    route(2 * i + s // 2, s % 2)
                    u_evac(i, s)
            own.wait(0)
            dve.sem_inc(routed, 1)
            own.done(dve.tensor_copy(den[:], tv[:, :, 0:1].rearrange("p a b -> p (a b)")))
            own.wait(0)
            dve.tensor_tensor(tv[:], tv[:], bcast(den[:], K16, 2), ALU.subtract).then_inc(top_ready, 1)
            for s in range(4):
                lo_next(U0, U1_ITERS, s)
                if s == 1:
                    dve.wait_ge(exp_done, 1)
                    own.done(dve.tensor_reduce(den[:], tv[:], AX.X, ALU.add))
                    own.wait(0)
                    own.done(dve.reciprocal(den[:], den[:]))
                    own.wait(0)
                    dve.tensor_tensor(gij[:, 0], tv[:], bcast(den[:], K16, 2), ALU.mult).then_inc(gate_w, 1)
                u_evac(U1_ITERS, s)

            def one_hots(gi, s):
                for b in range(2):
                    n = 2 * s + b
                    dve.wait_ge(g_done, 8 * gi + n + 1)
                    for t in range(4):
                        tok = 32 * gi + 4 * n + t
                        for part in range(2):
                            last = dve.tensor_scalar((ohB, ohL)[part][:, b, t, :], iota, gijT[:, 2, ds(tok, 1)],
                                                     ghl[:, part, ds(tok, 1)].bitcast(F32), ALU.is_equal, ALU.mult)
                    last.then_inc(oneB, 1)

            dve.wait_ge(gt_out, 4)
            own.done(dve.tensor_tensor(ghl[:, 1, :], gijT[:, 0, :], ghl[:, 0, :].bitcast(F32), ALU.subtract))
            own.wait(0)
            with dve.Fori(0, U2_ITERS) as i:
                for s in range(4):
                    lo_next(U0 + 4 * U2_0, i, s)
                    one_hots(i, s)
                    u_evac(i + U2_0, s)
            with dve.Fori(U2_0 + U2_ITERS, 31) as i:
                for s in range(4):
                    lo_next(U0, i, s)
                    u_evac(i, s)

            def product(b):
                dve.wait_ge(hg_in, 48 * (b + 1))
                hv = hin[:].rearrange("p j (t n) -> p t j n", t=TG)
                gv = gin[:].rearrange("p t (j n) -> p t j n", j=BLK)
                dve.tensor_tensor(hv, hv, gv, ALU.mult).then_inc(prod_done, 1)

            def act_lo(b, r):
                dve.wait_ge(ah_done, b + 1)
                dve.tensor_tensor(al[:, r], hin[:], ah[:, r].bitcast(F32), ALU.subtract).then_inc(act_ready, 1)

            for s in range(4):
                lo_next(U0, 31, s)
                if s == 0:
                    product(0)
                if s == 2:
                    act_lo(0, 0)
                u_evac(31, s)

            def v_iteration(i, last):
                for s in range(16):
                    if not (last and s == 15):
                        lo_next(V0, i, s, 16)
                    if not (last and s > 8):
                        if s % 8 == 2:
                            product(2 * i + s // 8 + 1)
                        if s % 8 == 4:
                            act_lo(2 * i + s // 8 + 1, (s // 8 + 1) % 2)
                    slot_ready(V0, i, s, 16)
                    for m in range(2):
                        t = hT[:, 2 * (s % 8) + m, :]
                        ins = dve.tensor_tensor(t, t, acc[:, 2 * (s % 2) + m, 0:N], ALU.add)
                    ins.then_inc(acc_free, 1)
                    dve.wait_ge(acc_free, slot_no(V0, i, s, 16) + 5) if s % 8 == 7 else None

            with dve.Fori(0, NBLK // 2 - 1) as i:
                v_iteration(i, False)
            v_iteration(NBLK // 2 - 1, True)
            norm_recip(4, 3)
            dve.wait_ge(fin_sq, 4)
            for t in range(DT):
                dve.scalar_tensor_tensor(hT[:, t, :], hT[:, t, :], par[:, Q_GFIN + t:Q_GFIN + t + 1], rstd[:, 0, :],
                                         ALU.mult, ALU.mult).then_inc(y_ready, 1)

        @block.tensor
        def _(pe):
            def product(out, w, mh, ml, n, before=None):
                wr, blocks = w
                for j in range(n):
                    if before:
                        before(j)
                    b = blocks(j)
                    pe.matmul(out, wh[:, wr, b, :], mh(j), start=(j == 0), stop=False)
                    pe.matmul(out, wh[:, wr, b, :], ml(j), start=False, stop=False)
                    ins = pe.matmul(out, wl[:, wr, b, :], mh(j), start=False, stop=(j == n - 1))
                return ins

            def slot(base, i, s, mh, ml, cols=N, before=None):
                g = slot_no(base, i, s)
                pe.wait_ge(lo_done, g + 1)
                pe.wait_ge(acc_free, g + 1)
                product(acc[:, s, 0:cols], (s % 2, lambda j: j), lambda j: mh[:, j, 0:cols], lambda j: ml[:, j, 0:cols],
                        DT, before).then_inc(slot_used, 1)

            def squares(n0, bank, cols):
                for c in range(8):
                    n = n0 + c
                    pe.wait_ge(sq_done, n + 1)
                    for j in range(2):
                        ins = pe.matmul(mis[:, bank, 0:cols], ones, sqb[:, n % 2, j, 0:cols], start=(c == 0 and j == 0), stop=(c == 7 and j == 1))
                    ins.then_inc(sq_used, 1)

            pe.sem_inc(g_done, 2)
            slot(MEM0, 0, 0, bh, bl, MEM, before=lambda j: pe.wait_ge(split_lo, j + 1))
            pe.wait_ge(const_in, 16)
            squares(0, 3, MEM)
            for s in range(1, 4):
                slot(MEM0, 0, s, bh, bl, MEM)
            slot(MEM0, 1, 0, bh, bl, MEM)
            squares(8, 2, N)
            for s in range(1, 4):
                slot(MEM0, 1, s, bh, bl, MEM)
            pe.wait_ge(split_lo, 2 * DT)
            with pe.Fori(0, 4) as i:
                for s in range(4):
                    slot(GLU0, i, s, xh, xl)
            with pe.Fori(0, 3) as i:
                for s in range(4):
                    slot(VKQ0, i, s, xh, xl)
            pe.wait_ge(rstd_done, 2)
            for h in range(2):
                for m in range(2):
                    for j in range(2):
                        ins = pe.transpose(mis[:, h, 256 * m + P * j:256 * m + P * j + P], mkvT[:, 4 + 2 * h + j, P * m:P * m + P], ident)
                ins.then_inc(vt_done, 1)
            pe.wait_ge(acc_free, VKQ0 + 4 + 12)
            for n, (bank, starts, ln) in enumerate(((0, (0, P), P), (1, (CHUNK,), P), (2, (P + CHUNK,), CHUNK), (3, (NP_,), NS))):
                if bank < 2:
                    pe.wait_ge(vt_out, bank + 1)
                for a, k0 in enumerate(starts):
                    for j in range(2):
                        ins = pe.transpose(mis[0:ln, bank, 256 * a + P * j:256 * a + P * j + P], kvT[:, j, k0:k0 + ln], ident)
                ins.then_inc(vt_done, 1)
            for j in range(10):
                pe.wait_ge(vt_out, 3 + j if j < 2 else 4)
                if j >= 2:
                    pe.wait_ge(rope_done, j - 1)
                if j < 2:
                    ins = pe.matmul(mis[:, j % 2, 0:N], rotm, kvT[:, 2 + j, :], start=True, stop=True)
                else:
                    pe.matmul(mis[:, j % 2, 0:NP_], rotm, qch[:, :, j - 2, :], start=True, stop=True)
                    ins = pe.matmul(mis[:, j % 2, NP_:N], rotm, qsm[:, j - 2, :], start=True, stop=True)
                ins.then_inc(rot_done, 1)

            def attention(A, hooks):
                S, units, n = A["sems"], A["units"], len(A["units"])
                for k in range(n + 3):
                    if k in hooks:
                        hooks[k]()
                    if k < n:
                        if k >= 2:
                            pe.wait_ge(S["prob"], k - 1)
                        for out, q, keys in A["scores"](k, units[k]):
                            ins = pe.matmul(out, q, keys, start=True, stop=True)
                        ins.then_inc(S["score"], 1)
                    if 0 <= k - 2 < n:
                        un, r = units[k - 2], (k - 2) % 3
                        R = un["rows"]
                        pe.wait_ge(S["norm"], k - 1)
                        if k >= 3:
                            pe.wait_ge(S["turnout"], k - 2)
                        for m, (a, ln, _) in enumerate(un["pieces"]):
                            for j in range(un["subs"]):
                                ins = pe.transpose(mis[0:ln, 2, 256 * m + P * j:256 * m + P * j + R],
                                                   prob[0:R, r, 256 * j + a:256 * j + a + ln], ident[0:R, 0:R])
                        ins.then_inc(S["turned"], 1)
                    if 0 <= k - 3 < n:
                        un = units[k - 3]
                        pe.wait_ge(S["turnout"], k - 2)
                        if k >= 4:
                            pe.wait_ge(S["vallo"], k - 3)
                        np_ = len(un["pieces"])
                        for j in range(un["subs"]):
                            for m in range(np_):
                                out, vals, pt = A["value"](un, j, m)
                                ins = pe.matmul(out, vals, pt, start=(m == 0), stop=(m == np_ - 1))
                        ins.then_inc(S["value"], 1)

            def ln_sum():
                pe.wait_ge(conv_pool, 1)
                pe.wait_ge(conv_dve, CT - 1)
                for t in range(CT):
                    ins = pe.matmul(acc[:, 0, 0:N], ones, y[:, t, :], start=(t == 0), stop=(t == CT - 1))
                ins.then_inc(ln_stat, 1)

            def ln_varf():
                for c in range(4):
                    pe.wait_ge(ln_sq, c + 1)
                    for j in range(2):
                        ins = pe.matmul(acc[:, 1, 0:N], ones, sqb[:, c % 2, j, :], start=(c == 0 and j == 0), stop=(c == 3 and j == 1))
                    ins.then_inc(ln_var, 1)

            pe.wait_ge(rope_done, 10)
            pe.wait_ge(vt_out, 6)
            pe.wait_ge(cache_in, 32)
            attention(SWA, {9: ln_sum, 12: ln_varf})
            pe.wait_ge(split_lo, 2 * DT + CT)
            pe.wait_ge(sw["vallo"], len(swa))
            with pe.Fori(0, 4) as i:
                for s in range(4):
                    slot(OUT0, i, s, xh, xl)

            def total(bank):
                pe.matmul(mis[:, bank, 0:N], ones, sqsum[:], start=True, stop=True).then_inc(stat_done, 1)

            pe.wait_ge(split_lo, 3 * DT + CT)
            for s in range(4):
                slot(CQ0, 0, s, bh, bl)
                if s == 0:
                    pe.wait_ge(sq_done, 17)
                    total(3)
            pe.wait_ge(acc_free, CO0 + 4)
            pe.wait_ge(rstd_done, 3)
            pe.wait_ge(smem_in, 32)
            attention(CROSS, {})
            pe.wait_ge(cr["vallo"], len(cross))
            for s in range(4):
                pe.wait_ge(lo_done, CO0 + s + 1)
                for m in range(4):
                    q = 4 * s + m
                    if q >= 4:
                        pe.wait_ge(co_free, q - 3)
                    product(acc[:, m, 0:N], (s % 2, lambda j, m=m: 4 * m + j), lambda j: ch[:, j, :], lambda j: cl[:, j, :],
                            MH).then_inc(co_done if m < 3 else slot_used, 1)
            pe.wait_ge(split_lo, 4 * DT + CT)
            pe.wait_ge(co_free, DT)

            def pq(i, first):
                for s in range(4):
                    slot(PQ0, i, s, xh, xl)
                    if first and s == 0:
                        pe.wait_ge(sq_done, 18)
                        total(2)
                        pe.wait_ge(sk_in, 16)
                    if s > 0:
                        scores(i, s - 1, first)
                scores(i, 3, first)

            def scores(i, s, first):
                pe.wait_ge(acc_free, slot_no(PQ0, i, s) + 5)
                if not (first and s < 2):
                    pe.wait_ge(pq_out, 4 * i + s - 1)
                for t in range(3):
                    R = P if t < 2 else NS
                    ins = pe.matmul(mis[0:R, s % 2, P * t:P * t + P], qp[:, s % 2, P * t:P * t + R],
                                    skT[:, ds(4 * i + s, 1), :].rearrange("p a c -> p (a c)"), start=True, stop=True)
                ins.then_inc(pq_score, 1)

            pq(0, True)
            with pe.Fori(1, 4) as i:
                pq(i, False)
            with pe.Fori(0, U1_ITERS + 1) as i:
                for s in range(4):
                    slot(U0, i, s, xh, xl)
            pe.wait_ge(gate_w, 1)
            pe.wait_ge(rstd_done, 4)
            pe.wait_ge(pq_out, 16)
            for n in range(3):
                for t in range(3):
                    R = P if t < 2 else NS
                    src = gij[0:R, n, 8 * t:8 * t + 8, :].rearrange("p h r -> p (h r)")
                    ins = pe.transpose(mis[:, n, P * t:P * t + R], src, ident[0:R, 0:R])
                ins.then_inc(gt_done, 1)
            pe.wait_ge(gt_out, 4)
            with pe.Fori(0, U2_ITERS) as i:
                for s in range(4):
                    slot(U0 + 4 * U2_0, i, s, xh, xl)
                    for b in range(2):
                        n = 8 * i + 2 * s + b
                        pe.wait_ge(oneA, n + 1)
                        pe.wait_ge(oneB, n + 1)
                        pe.wait_ge(g_evac, n + 1)
                        for t in range(4):
                            pe.matmul(mis[:, b, P * t:P * t + P], ohA[:, b, t, :], ohB[:, b, t, :], start=True, stop=False)
                            ins = pe.matmul(mis[:, b, P * t:P * t + P], ohA[:, b, t, :], ohL[:, b, t, :], start=False, stop=True)
                        ins.then_inc(g_done, 1)
            with pe.Fori(U2_0 + U2_ITERS, 32) as i:
                for s in range(4):
                    slot(U0, i, s, xh, xl)
            with pe.Fori(0, NBLK // 2) as i:
                for s in range(16):
                    g = slot_no(V0, i, s, 16)
                    r = s // 8
                    if s % 8 == 0:
                        pe.wait_ge(act_ready, 2 * i + r + 1)
                    pe.wait_ge(lo_done, g + 1)
                    pe.wait_ge(acc_free, g + 3)
                    for m in range(2):
                        ins = product(acc[:, 2 * (s % 2) + m, 0:N], (s % 2, lambda j, m=m: BLK * m + j),
                                      lambda j: ah[:, r, j, :], lambda j: al[:, r, j, :], BLK)
                    ins.then_inc(slot_used, 1)
            for n in range(4):
                pe.wait_ge(fin_sq, n + 1)
                for j in range(4):
                    ins = pe.matmul(mis[:, 3, 0:N], ones, hin[:, 4 * (n % 2) + j, :], start=(n == 0 and j == 0), stop=(n == 3 and j == 3))
                ins.then_inc(fin_used if n < 3 else stat_done, 1)

        @block.gpsimd
        def _(pool):
            own = Own(pool, pool_own)

            def one(ap):
                return ap.rearrange("p a n -> p (a n)")

            pool.wait_ge(par_in, 16)
            for n in range(16):
                src = (memT, hT)[n // 8][:, 2 * (n % 8):2 * (n % 8) + 2, :]
                if n < 8 and n % 2 == 0:
                    pool.wait_ge(mem_in[n // 2], 16)
                if n == 8:
                    pool.wait_ge(x_in, 16)
                if n >= 2:
                    pool.wait_ge(sq_used, n - 1)
                pool.tensor_tensor(sqb[:, n % 2, :, 0:src.shape[2]], src, src, ALU.mult).then_inc(sq_done, 1)
            pool.wait_ge(slot_used, 8)
            pool.memset(glu[:, :, 0:HIST], 0.0).then_inc(hist_zero, 1)
            pool.dma_start(glu[:, :, S0:S0 + HIST], dr["cconv"]).then_inc(hist_in, 16)
            pool.dma_start(ckT[:], dr["ckT"]).then_inc(cache_in, 16)
            pool.dma_start(vtok[:, 5, :], dr["cv"]).then_inc(cache_in, 16)
            pool.wait_ge(acc_free, 12)
            pool.dma_start(dr["mkvT"], mkvT[:]).then_inc(early_out, 16)
            with pool.Fori(0, 4) as i:
                for s in range(2):
                    n = 2 * i + s
                    pool.wait_ge(sig_done, n + 1)
                    pool.wait_ge(acc_free, GLU0 + 4 + 2 * n)
                    if s == 0:
                        pool.wait_ge(rstd_done, 2)
                    pool.tensor_tensor(gsb[:, 2, :], gsb[:, 1, :], rstd[:, 1, :], ALU.mult).then_inc(sgr_done, 1)
            pool.wait_ge(acc_free, VKQ0 + 4)
            pool.wait_ge(hist_zero, 1)
            pool.wait_ge(hist_in, 16)
            pool.dma_start(dr["nconv_p"], glu[:, :, NP_:NP_ + HIST]).then_inc(early_out, 16)
            pool.dma_start(dr["nconv_s"], glu[:, :, XW - HIST:XW]).then_inc(early_out, 16)
            ct = CT - 1
            for n in range(TAPS):
                w = par[:, Q_CW + TAPS * ct + n:Q_CW + TAPS * ct + n + 1]
                x = glu[:, ct, n:n + YW]
                if n == 0:
                    own.done(pool.tensor_scalar(pacc[:, 0, :], x, w, par[:, Q_CB + ct:Q_CB + ct + 1], ALU.mult, ALU.add))
                    continue
                own.wait(0)
                own.done(pool.tensor_scalar(pacc[:, 1, :], x, w, None, ALU.mult))
                own.wait(0)
                own.done(pool.tensor_tensor(pacc[:, 0, :], pacc[:, 0, :], pacc[:, 1, :], ALU.add))
            own.wait(0)
            own.done(pool.tensor_copy(y[:, ct, 0:NP_], pacc[:, 0, 0:NP_]))
            pool.tensor_copy(y[:, ct, NP_:N], pacc[:, 0, S0:YW]).then_inc(conv_pool, 1)
            pool.wait_ge(rope_done, 2)
            pool.dma_start(dr["nkv_p"], kvT[:, 0:4, P:NP_]).then_inc(early_out, 16)
            pool.dma_start(dr["nkv_s"], kvT[:, 0:4, NP_:N]).then_inc(early_out, 16)
            pool.wait_ge(cache_in, 32)
            pool.dma_start(dr["nk_old"], ckT[:, :, NS:WINDOW]).then_inc(early_out, 16)
            pool.dma_start(dr["nv_old"], vtok[NS:WINDOW, 5, :]).then_inc(early_out, 16)
            pool.wait_ge(ln_var, 4)
            pool.dma_start(smkT[:], dr["smkT"]).then_inc(smem_in, 16)
            pool.dma_start(smv[:], dr["smv"]).then_inc(smem_in, 16)
            pool.wait_ge(ln_scaled, 1)
            own.done(pool.memset(sqsum[:], 0.0))
            with pool.Fori(0, 4) as i, own.loop(i, 0, 4, 8):
                for s in range(4):
                    t = one(hT[:, ds(4 * i + s, 1), :])
                    pool.wait_ge(acc_free, slot_no(OUT0, i, s) + 5)
                    own.wait(0)
                    own.done(pool.tensor_tensor(sqt[:], t, t, ALU.mult))
                    own.wait(0)
                    own.done(pool.tensor_tensor(sqsum[:], sqsum[:], sqt[:], ALU.add))
            own.wait(0)
            pool.sem_inc(sq_done, 1)
            pool.wait_ge(stat_done, 1)
            own.done(pool.memset(sqsum[:], 0.0))
            pool.wait_ge(slot_used, CO0)
            pool.dma_start(skT[:], dr["skT"]).then_inc(sk_in, 16)
            for m in range(DT):
                pool.wait_ge(co_free, m + 1)
                own.wait(0)
                own.done(pool.tensor_tensor(sqt[:], hT[:, m, :], hT[:, m, :], ALU.mult))
                own.wait(0)
                own.done(pool.tensor_tensor(sqsum[:], sqsum[:], sqt[:], ALU.add))
            own.wait(0)
            pool.sem_inc(sq_done, 1)
            pool.wait_ge(slot_used, PQ0)
            pool.memset(stok[:, 16:24], 0.0).then_inc(stok_zero, 1)
            pool.wait_ge(const_in, 16)
            pool.wait_ge(gt_out, 3)
            with pool.Fori(0, U2_ITERS) as i:
                pool.wait_ge(g_done, 8 * i + 2)
                pool.tensor_copy(tok32[:], gijT[:, 1, ds(32 * i, 32)]).then_inc(tok_in, 1)
                pool.wait_ge(tok_in, i + 1)
                for s in range(4):
                    for b in range(2):
                        n = 2 * s + b
                        pool.wait_ge(g_done, 8 * i + n + 1)
                        pool.nop(nofuse=True)
                        for t in range(4):
                            last = pool.tensor_scalar(ohA[:, b, t, :], iota, tok32[:, 4 * n + t:4 * n + t + 1], None, ALU.is_equal)
                        last.then_inc(oneA, 1)




def slots(w):
    k, m = w.shape
    return np.ascontiguousarray(w.reshape(k // P, P, m // P, P).transpose(2, 1, 0, 3))


def tiles(x):
    n, d = x.shape
    return np.ascontiguousarray(x.reshape(n, d // P, P).transpose(2, 1, 0))


def columns(x):
    return np.ascontiguousarray(x.reshape(-1, P).T)


def constants():
    c = np.zeros((P, C_W), np.float32)
    c[:, C_ID:C_ID + P] = np.eye(P)
    c[:, C_ONE:C_ONE + P] = 1
    c[:, C_IOTA:C_IOTA + P] = np.arange(P)
    half = ROT // 2
    inv = np.power(np.float32(THETA), -(np.float32(2.0) * np.arange(half, dtype=np.float32)) / np.float32(ROT)).astype(np.float32)
    pos = np.concatenate([np.arange(NP_), PAST + np.arange(NS)]).astype(np.float32)
    ang = (pos[None, :] * inv[:, None]).astype(np.float32)
    c[:, C_COS:C_COS + N] = 1
    for h in range(P // HD):
        for r in range(half):
            a, b = h * HD + r, h * HD + half + r
            c[b, C_ROT + a] = -1
            c[a, C_ROT + b] = 1
            for row in (a, b):
                c[row, C_COS:C_COS + N] = np.cos(ang[r])
                c[row, C_SIN:C_SIN + N] = np.sin(ang[r])
    return c


def kernel(x_prompt, x_sample, mem_prompt, cache_conv, cache_swa_k, cache_swa_v, cache_mem_k, cache_mem_v,
           norm_mix_g, w_in, conv_dw_w, conv_dw_b, conv_ln_g, conv_ln_b, swa_sinks, w_out,
           norm_cross_g, norm_mem_g, w_cq, w_ck, w_cv, w_co,
           norm_ffn_g, peer_wq, peer_subkeys, peer_u, peer_v, norm_final_g):
    import concourse.bacc as bacc
    from concourse.bass_utils import run_bass_kernel_spmd

    (x_prompt, x_sample, mem_prompt, cache_conv, cache_swa_k, cache_swa_v, cache_mem_k, cache_mem_v,
     norm_mix_g, w_in, conv_dw_w, conv_dw_b, conv_ln_g, conv_ln_b, swa_sinks, w_out,
     norm_cross_g, norm_mem_g, w_cq, w_ck, w_cv, w_co, norm_ffn_g, peer_wq, peer_subkeys, peer_u, peer_v,
     norm_final_g) = [np.asarray(a) for a in (
         x_prompt, x_sample, mem_prompt, cache_conv, cache_swa_k, cache_swa_v, cache_mem_k, cache_mem_v,
         norm_mix_g, w_in, conv_dw_w, conv_dw_b, conv_ln_g, conv_ln_b, swa_sinks, w_out,
         norm_cross_g, norm_mem_g, w_cq, w_ck, w_cv, w_co, norm_ffn_g, peer_wq, peer_subkeys, peer_u, peer_v,
         norm_final_g)]
    order = [HD * h + d for t in range(8) for h in (8 * (t // 4) + t % 4, 8 * (t // 4) + t % 4 + 4) for d in range(HD)]
    w = w_in[0]
    a, q, k, v = w[:, :2 * CONV], w[:, 2 * CONV:2 * CONV + 1024], w[:, 3072:3328], w[:, 3328:]
    glu = slots(a).reshape(2, CT, P, DT, P)[::-1].transpose(1, 0, 2, 3, 4).reshape(2 * CT, P, DT, P)
    w_mix = np.concatenate([glu, slots(v), slots(k), slots(q[:, order])])
    wo = w_out[0]
    sink = swa_sinks[0].reshape(4, 4)
    sink_p = np.repeat(sink.reshape(4, 2, 2).transpose(2, 0, 1).reshape(2, 8), CHUNK, axis=0)
    sink_s = np.repeat(sink.T, NS, axis=0)
    par = np.concatenate(
        [columns(norm_mix_g[0]), columns(norm_cross_g[0]), columns(norm_mem_g[0]), columns(norm_ffn_g[0]),
         columns(norm_final_g), conv_dw_w[0].reshape(TAPS, CT, P).transpose(2, 1, 0).reshape(P, CT * TAPS),
         columns(conv_dw_b[0]), columns(conv_ln_g[0]), columns(conv_ln_b[0]), sink_p, sink_s], axis=1)
    host = {
        "cst": constants(), "par": par,
        "xT": np.concatenate([tiles(x_prompt[0]), tiles(x_sample[0])], axis=2), "memT": tiles(mem_prompt[0]),
        "w_mem": np.concatenate([slots(w_ck[0]), slots(w_cv[0])]), "w_mix": w_mix,
        "w_out": slots(np.concatenate([wo[:CONV], wo[CONV:][order]])), "w_cq": slots(w_cq[0]),
        "w_co": w_co[0].reshape(MH, P, 4, 4, P).transpose(2, 1, 3, 0, 4).reshape(4, P, DT, P),
        "w_pq": slots(peer_wq[0]), "u": peer_u[0].reshape(P, P, DT, P).transpose(1, 3, 2, 0),
        "v": peer_v[0].reshape(P, NBLK, BLK, 8, 2, P).transpose(1, 3, 0, 4, 2, 5).reshape(P, P, DT, P),
        "cconv": tiles(cache_conv[0, 0]), "ckT": tiles(cache_swa_k[0, 0].reshape(WINDOW, 256)),
        "cv": cache_swa_v[0, 0].reshape(WINDOW, 256), "smkT": tiles(cache_mem_k[0, 0].reshape(MEM, MH * P)),
        "smv": cache_mem_v[0, 0].reshape(2, P, MH * P).transpose(1, 0, 2),
        "skT": peer_subkeys[0].reshape(16, NKEYS, P).transpose(2, 0, 1)}
    outs = {"yT": (P, DT, N), "mkvT": (P, 8, MEM), "nconv_p": (P, CT, HIST), "nconv_s": (P, CT, HIST),
            "nkv_p": (P, 4, P), "nkv_s": (P, 4, NS), "nk_old": (P, 2, WINDOW - NS), "nv_old": (WINDOW - NS, 256)}
    nc = bacc.Bacc("TRN2", target_bir_lowering=False, num_devices=1)
    host = {n: np.ascontiguousarray(x) for n, x in host.items()}
    dr = {n: nc.dram_tensor("in_" + n, x.shape, F32, kind="ExternalInput").ap() for n, x in host.items()}
    for n, shape in outs.items():
        dr[n] = nc.dram_tensor("out_" + n, shape, F32, kind="ExternalOutput").ap()
    dr["h"] = nc.dram_tensor("h", (32, P, 4, N), F32, kind="Internal").ap()
    dr["G"] = nc.dram_tensor("G", (NBLK, P, TG, BLK * 16), F32, kind="Internal").ap()
    build(nc, dr)
    r = run_bass_kernel_spmd(nc, [{"in_" + n: x for n, x in host.items()}], core_ids=[0]).results[0]
    o = {n: np.asarray(r["out_" + n]) for n in outs}

    def rows(t):
        return np.ascontiguousarray(t.transpose(2, 1, 0).reshape(t.shape[2], -1))

    y = rows(o["yT"])
    mk, mv = rows(o["mkvT"][:, 0:4]), rows(o["mkvT"][:, 4:8])
    vp, kp = rows(o["nkv_p"][:, 0:2]), rows(o["nkv_p"][:, 2:4])
    vs = np.concatenate([o["nv_old"], rows(o["nkv_s"][:, 0:2])])
    ks = np.concatenate([rows(o["nk_old"]), rows(o["nkv_s"][:, 2:4])])
    kv, mem = (1, 1, WINDOW, 4, HD), (1, 1, MEM, MH, P)
    return (y[:NP_].reshape(1, NP_, D), y[NP_:].reshape(1, NS, D), rows(o["nconv_p"]).reshape(1, 1, HIST, CONV),
            kp.reshape(kv), vp.reshape(kv), mk.reshape(mem), mv.reshape(mem),
            rows(o["nconv_s"]).reshape(1, 1, HIST, CONV), ks.reshape(kv), vs.reshape(kv))
```
